# Optimizing a Trainium2 kernel written in Bass

```python
import jax, jax.numpy as jnp
from jax import lax
import numpy as np

D_MODEL = 1024
BATCH = 1
SEQ = 1024
DEPTH = 1

N_MIXERS = 2
N_HGRN_LAYERS = (DEPTH + N_MIXERS - 1) // N_MIXERS
N_ATTN_LAYERS = (DEPTH - 1 + N_MIXERS - 1) // N_MIXERS

HGRN_HEAD_DIM = 128
HGRN_HEADS = D_MODEL // HGRN_HEAD_DIM
HGRN_CHUNK = 64

ATTN_HEADS = 16
ATTN_HEAD_DIM = D_MODEL // ATTN_HEADS
DILATED_GROUPS = ((128, 1), (512, 4), (2048, 16))
N_GROUPS = len(DILATED_GROUPS)
ATTN_BLOCK = 128

MLP_HIDDEN = 4 * D_MODEL
NORM_EPS = 1e-6


def _rmsnorm(x, gain):
    xf = x.astype(jnp.float32)
    y = xf * lax.rsqrt(jnp.mean(xf * xf, axis=-1, keepdims=True) + NORM_EPS)
    return (y * gain.astype(jnp.float32)).astype(x.dtype)

def _hgrn2_chunk_scan(q, k, v, log_f):
    b, s, h, dk = q.shape
    dv = v.shape[-1]
    nc = s // HGRN_CHUNK

    def to_chunks(t):
        return t.reshape(b, nc, HGRN_CHUNK, h, t.shape[-1]).transpose(1, 0, 3, 2, 4)

    causal = jnp.tril(jnp.ones((HGRN_CHUNK, HGRN_CHUNK), dtype=bool))

    def step(state, inp):
        qi, ki, vi, gi = inp
        cum = jnp.cumsum(gi, axis=2)
        o_inter = jnp.einsum('bhtk,bhkv->bhtv', qi * jnp.exp(cum), state)
        diff = cum[:, :, :, None, :] - cum[:, :, None, :, :]
        decay = jnp.exp(jnp.where(causal[:, :, None], diff, -jnp.inf))
        scores = jnp.einsum('bhtk,bhtsk,bhsk->bhts', qi, decay, ki)
        o_intra = jnp.einsum('bhts,bhsv->bhtv', scores, vi)
        last = cum[:, :, -1:, :]
        k_dec = ki * jnp.exp(last - cum)
        new_state = (jnp.exp(last[:, :, 0, :])[..., None] * state
                     + jnp.einsum('bhsk,bhsv->bhkv', k_dec, vi))
        return new_state, o_inter + o_intra

    init = jnp.zeros((b, h, dk, dv), jnp.float32)
    _, o = lax.scan(step, init, (to_chunks(q), to_chunks(k), to_chunks(v), to_chunks(log_f)))
    return o.transpose(1, 0, 3, 2, 4).reshape(b, s, h, dv)

def _hgrn2_mixer(h, w_in, lower_bound, out_norm, w_out):
    b, s, _ = h.shape
    proj = h @ w_in
    q, f, i, g = jnp.split(proj, 4, axis=-1)
    ff = f.astype(jnp.float32)
    lb = lower_bound.astype(jnp.float32)
    log_f = jnp.logaddexp(jnp.log(lb), jnp.log1p(-lb) + jax.nn.log_sigmoid(ff))
    k = (1.0 - lb) * jax.nn.sigmoid(-ff)
    qf = jax.nn.silu(q.astype(jnp.float32)) * (HGRN_HEAD_DIM ** -0.5)
    heads = lambda t: t.reshape(b, s, HGRN_HEADS, HGRN_HEAD_DIM)
    o = _hgrn2_chunk_scan(heads(qf), heads(k), heads(i.astype(jnp.float32)), heads(log_f))
    o = o * lax.rsqrt(jnp.mean(o * o, axis=-1, keepdims=True) + NORM_EPS)
    o = o.reshape(b, s, D_MODEL) * out_norm.astype(jnp.float32) * jax.nn.silu(g.astype(jnp.float32))
    return o.astype(h.dtype) @ w_out

def _banded_causal_attention(q, k, v, reach):
    n, l, h, dh = q.shape
    blk = ATTN_BLOCK
    nb = -(-l // blk)
    lp = nb * blk
    qb = jnp.pad(q, ((0, 0), (0, lp - l), (0, 0), (0, 0))).reshape(n, nb, blk, h, dh)
    pad_kv = ((0, 0), (blk, lp - l), (0, 0), (0, 0))
    kp = jnp.pad(k, pad_kv).reshape(n, nb + 1, blk, h, dh)
    vp = jnp.pad(v, pad_kv).reshape(n, nb + 1, blk, h, dh)
    kb = jnp.concatenate([kp[:, :-1], kp[:, 1:]], axis=2)
    vb = jnp.concatenate([vp[:, :-1], vp[:, 1:]], axis=2)
    bidx = jnp.arange(nb)[:, None, None]
    qpos = bidx * blk + jnp.arange(blk)[None, :, None]
    kpos = (bidx - 1) * blk + jnp.arange(2 * blk)[None, None, :]
    dist = qpos - kpos
    mask = (kpos >= 0) & (dist >= 0) & (dist <= reach)
    s = jnp.einsum('nbqhd,nbkhd->nbhqk', qb, kb).astype(jnp.float32) * (dh ** -0.5)
    s = jnp.where(mask[None, :, None], s, -jnp.inf)
    lse = jax.nn.logsumexp(s, axis=-1)
    p = jnp.exp(s - lse[..., None])
    o = jnp.einsum('nbhqk,nbkhd->nbqhd', p.astype(v.dtype), vb).astype(jnp.float32)
    o = o.reshape(n, lp, h, dh)[:, :l]
    lse = lse.transpose(0, 1, 3, 2).reshape(n, lp, h)[:, :l]
    return o, lse

def _dilated_group(q, k, v, dilation, reach):
    b, s, h, dh = q.shape
    l = s // dilation

    def split(t):
        return t.reshape(b, l, dilation, h, dh).transpose(0, 2, 1, 3, 4).reshape(b * dilation, l, h, dh)

    o, lse = _banded_causal_attention(split(q), split(k), split(v), reach)
    o = o.reshape(b, dilation, l, h, dh).transpose(0, 2, 1, 3, 4).reshape(b, s, h, dh)
    lse = lse.reshape(b, dilation, l, h).transpose(0, 2, 1, 3).reshape(b, s, h)
    return o, lse

def _dilated_attention_mixer(h, w_qkv, w_out):
    b, s, _ = h.shape
    proj = (h @ w_qkv).reshape(b, s, N_GROUPS, 3, ATTN_HEADS, ATTN_HEAD_DIM)
    outs, lses = [], []
    for g, (window, dilation) in enumerate(DILATED_GROUPS):
        o, lse = _dilated_group(proj[:, :, g, 0], proj[:, :, g, 1], proj[:, :, g, 2],
                                dilation, window // dilation)
        outs.append(o)
        lses.append(lse)
    weights = jax.nn.softmax(jnp.stack(lses, axis=0), axis=0)
    o = jnp.sum(weights[..., None] * jnp.stack(outs, axis=0), axis=0)
    return o.reshape(b, s, D_MODEL).astype(h.dtype) @ w_out

def _squared_relu_mlp(h, w1, w2):
    a = jax.nn.relu(h @ w1)
    return (a * a) @ w2

def first_inputs(seed: int = 0) -> dict:
    key = jax.random.key(seed)
    ks = jax.random.split(key, 13)
    nrm = lambda k, shape: jax.random.normal(k, shape, jnp.float32)
    d = D_MODEL
    return {
        "x": nrm(ks[0], (BATCH, SEQ, d)),
        "norm_mix": 1.0 + 0.02 * nrm(ks[1], (DEPTH, d)),
        "norm_mlp": 1.0 + 0.02 * nrm(ks[2], (DEPTH, d)),
        "norm_final": 1.0 + 0.02 * nrm(ks[3], (d,)),
        "hgrn_w_in": nrm(ks[4], (N_HGRN_LAYERS, d, 4 * d)) * d ** -0.5,
        "hgrn_lower_bound": 0.5 * nrm(ks[5], (N_HGRN_LAYERS, d)),
        "hgrn_out_norm": 1.0 + 0.02 * nrm(ks[6], (N_HGRN_LAYERS, d)),
        "hgrn_w_out": nrm(ks[7], (N_HGRN_LAYERS, d, d)) * d ** -0.5,
        "attn_w_qkv": nrm(ks[8], (N_ATTN_LAYERS, d, N_GROUPS * 3 * d)) * d ** -0.5,
        "attn_w_out": nrm(ks[9], (N_ATTN_LAYERS, d, d)) * d ** -0.5,
        "mlp_w1": nrm(ks[10], (DEPTH, d, MLP_HIDDEN)) * d ** -0.5,
        "mlp_w2": nrm(ks[11], (DEPTH, MLP_HIDDEN, d)) * MLP_HIDDEN ** -0.5,
    }

def first_block(x, norm_mix, norm_mlp, norm_final, hgrn_w_in, hgrn_lower_bound, hgrn_out_norm,
              hgrn_w_out, attn_w_qkv, attn_w_out, mlp_w1, mlp_w2):
    lb_all = jnp.cumsum(jax.nn.softmax(hgrn_lower_bound.astype(jnp.float32), axis=0), axis=0)
    lb_all = lb_all - lb_all[0]
    for layer in range(DEPTH):
        j = layer // N_MIXERS
        h = _rmsnorm(x, norm_mix[layer])
        if layer % N_MIXERS == 0:
            mix = _hgrn2_mixer(h, hgrn_w_in[j], lb_all[j], hgrn_out_norm[j], hgrn_w_out[j])
        else:
            mix = _dilated_attention_mixer(h, attn_w_qkv[j], attn_w_out[j])
        x = x + mix
        x = x + _squared_relu_mlp(_rmsnorm(x, norm_mlp[layer]), mlp_w1[layer], mlp_w2[layer])
    return _rmsnorm(x, norm_final)


MIX_WIDTH = D_MODEL
CONV_WIDTH = MIX_WIDTH // 2
CONV_GROUPS = 8
CONV_K = 3
RET_WIDTH = MIX_WIDTH - CONV_WIDTH
RET_HEADS = 4
RET_HEAD_DIM = RET_WIDTH // RET_HEADS
RET_CHUNK = 128
ROPE_BASE = 10000.0
D_FF = 4 * D_MODEL
IN_COLS = 3 * CONV_WIDTH + 4 * RET_WIDTH


def rms_norm(x, g, eps=NORM_EPS):
    xf = x.astype(jnp.float32)
    y = xf * lax.rsqrt(jnp.mean(xf * xf, axis=-1, keepdims=True) + eps)
    return (y * g.astype(jnp.float32)).astype(x.dtype)

def group_rms_norm(x, g, n_groups, eps=NORM_EPS):
    shp = x.shape
    xg = x.reshape(shp[:-1] + (n_groups, shp[-1] // n_groups)).astype(jnp.float32)
    y = xg * lax.rsqrt(jnp.mean(xg * xg, axis=-1, keepdims=True) + eps)
    return (y.reshape(shp) * g.astype(jnp.float32)).astype(x.dtype)

def rotary(x, positions):
    half = x.shape[-1] // 2
    inv_freq = 1.0 / (ROPE_BASE ** (jnp.arange(half, dtype=jnp.float32) / half))
    ang = positions.astype(jnp.float32)[:, None] * inv_freq[None, :]
    cos = jnp.cos(ang)[None, :, None, :].astype(x.dtype)
    sin = jnp.sin(ang)[None, :, None, :].astype(x.dtype)
    x1, x2 = x[..., :half], x[..., half:]
    return jnp.concatenate([x1 * cos - x2 * sin, x2 * cos + x1 * sin], axis=-1)

def causal_dwconv3(u, w):
    up = jnp.pad(u, ((0, 0), (CONV_K - 1, 0), (0, 0)))
    s = u.shape[1]
    return up[:, 0:s] * w[0] + up[:, 1:s + 1] * w[1] + up[:, 2:s + 2] * w[2]

def chunkwise_retention(q, k, v):
    b, s, h, d = q.shape
    nc = s // RET_CHUNK
    dt = q.dtype
    to_chunks = lambda t: t.reshape(b, nc, RET_CHUNK, h, d).transpose(0, 3, 1, 2, 4)
    qc, kc, vc = to_chunks(q), to_chunks(k), to_chunks(v)

    log_gamma = jnp.log(1.0 - 2.0 ** (-5.0 - jnp.arange(h, dtype=jnp.float32)))
    idx = jnp.arange(RET_CHUNK, dtype=jnp.float32)
    diff = idx[:, None] - idx[None, :]
    intra_decay = jnp.where(diff[None] >= 0,
                            jnp.exp(log_gamma[:, None, None] * jnp.maximum(diff, 0.0)[None]),
                            0.0).astype(dt)
    zeta = jnp.exp(log_gamma[:, None] * (RET_CHUNK - 1 - idx)[None]).astype(dt)
    xi = jnp.exp(log_gamma[:, None] * (idx + 1.0)[None]).astype(dt)
    chunk_decay = jnp.exp(log_gamma * RET_CHUNK).astype(dt)

    scores = jnp.einsum('bhncd,bhnmd->bhncm', qc, kc) * intra_decay[None, :, None]
    o_intra = jnp.einsum('bhncm,bhnme->bhnce', scores, vc)

    kv = jnp.einsum('bhnmd,bhnme->nbhde', kc * zeta[None, :, None, :, None], vc)

    def step(state, kv_n):
        new_state = chunk_decay[None, :, None, None] * state + kv_n
        return new_state, state

    _, s_prev = lax.scan(step, jnp.zeros_like(kv[0]), kv)
    o_cross = jnp.einsum('bhncd,nbhde->bhnce', qc * xi[None, :, None, :, None], s_prev)

    o = o_intra + o_cross
    return o.transpose(0, 2, 3, 1, 4).reshape(b, s, h, d)

def hybrid_mixer(u, w_in, conv_w, conv_norm_g, ret_norm_g, w_out):
    b, s, _ = u.shape
    z = u @ w_in
    c0 = 3 * CONV_WIDTH
    cb, cc, ch = jnp.split(z[..., :c0], 3, axis=-1)
    rq, rk, rv, rg = jnp.split(z[..., c0:], 4, axis=-1)

    y_conv = cb * causal_dwconv3(cc * ch, conv_w)
    y_conv = group_rms_norm(y_conv, conv_norm_g, CONV_GROUPS)

    positions = jnp.arange(s)
    q = rotary(rq.reshape(b, s, RET_HEADS, RET_HEAD_DIM), positions)
    k = rotary(rk.reshape(b, s, RET_HEADS, RET_HEAD_DIM), positions) * (RET_HEAD_DIM ** -0.5)
    v = rv.reshape(b, s, RET_HEADS, RET_HEAD_DIM)
    o = chunkwise_retention(q, k, v).reshape(b, s, RET_WIDTH)
    y_ret = group_rms_norm(o, ret_norm_g, RET_HEADS) * jax.nn.silu(rg)

    return jnp.concatenate([y_conv, y_ret], axis=-1) @ w_out

def sq_relu_mlp(u, w_up, w_down):
    hdn = jax.nn.relu(u @ w_up)
    return (hdn * hdn) @ w_down

def second_inputs(seed: int = 0) -> dict:
    key = jax.random.key(seed)
    ks = jax.random.split(key, 11)
    f32 = jnp.float32
    x = jax.random.normal(ks[0], (BATCH, SEQ, D_MODEL), f32)
    norm1_g = 1.0 + 0.05 * jax.random.normal(ks[1], (D_MODEL,), f32)
    w_in = jax.random.normal(ks[2], (D_MODEL, IN_COLS), f32) * D_MODEL ** -0.5
    conv_w = jax.random.normal(ks[3], (CONV_K, CONV_WIDTH), f32) * CONV_K ** -0.5
    conv_norm_g = 1.0 + 0.05 * jax.random.normal(ks[4], (CONV_WIDTH,), f32)
    ret_norm_g = 1.0 + 0.05 * jax.random.normal(ks[5], (RET_WIDTH,), f32)
    w_out = jax.random.normal(ks[6], (MIX_WIDTH, D_MODEL), f32) * MIX_WIDTH ** -0.5
    norm2_g = 1.0 + 0.05 * jax.random.normal(ks[7], (D_MODEL,), f32)
    w_up = jax.random.normal(ks[8], (D_MODEL, D_FF), f32) * D_MODEL ** -0.5
    w_down = jax.random.normal(ks[9], (D_FF, D_MODEL), f32) * D_FF ** -0.5
    final_norm_g = 1.0 + 0.05 * jax.random.normal(ks[10], (D_MODEL,), f32)
    return {"x": x, "norm1_g": norm1_g, "w_in": w_in, "conv_w": conv_w,
            "conv_norm_g": conv_norm_g, "ret_norm_g": ret_norm_g, "w_out": w_out,
            "norm2_g": norm2_g, "w_up": w_up, "w_down": w_down,
            "final_norm_g": final_norm_g}

def second_block(x, norm1_g, w_in, conv_w, conv_norm_g, ret_norm_g, w_out,
              norm2_g, w_up, w_down, final_norm_g):
    h = x
    for _ in range(DEPTH):
        h = h + hybrid_mixer(rms_norm(h, norm1_g), w_in, conv_w, conv_norm_g, ret_norm_g, w_out)
        h = h + sq_relu_mlp(rms_norm(h, norm2_g), w_up, w_down)
    return rms_norm(h, final_norm_g)


def setup_inputs(seed=0):
    out = dict(first_inputs(seed))
    for name, value in second_inputs(seed + 1).items():
        if name != "x":
            out[name + "_2"] = value
    return out


def reference(
    x, norm_mix, norm_mlp, norm_final, hgrn_w_in, hgrn_lower_bound, hgrn_out_norm, hgrn_w_out,
    attn_w_qkv, attn_w_out, mlp_w1, mlp_w2, norm1_g_2, w_in_2, conv_w_2, conv_norm_g_2,
    ret_norm_g_2, w_out_2, norm2_g_2, w_up_2, w_down_2, final_norm_g_2,
):
    x = first_block(
        x, norm_mix, norm_mlp, norm_final, hgrn_w_in, hgrn_lower_bound, hgrn_out_norm,
        hgrn_w_out, attn_w_qkv, attn_w_out, mlp_w1, mlp_w2,
    )
    return second_block(
        x, norm1_g_2, w_in_2, conv_w_2, conv_norm_g_2, ret_norm_g_2, w_out_2, norm2_g_2, w_up_2,
        w_down_2, final_norm_g_2,
    )


_drawn_inputs = setup_inputs


def setup_inputs(seed=0):
    import zlib

    import numpy as np

    out = dict(_drawn_inputs(seed))
    spreads = {}
    factors = {'hgrn_out_norm': 3.254, 'ret_norm_g_2': 3.215, 'norm_mlp': 2.721, 'conv_norm_g_2': 2.883}
    for name, (base, spread) in spreads.items():
        noise = np.random.default_rng([zlib.crc32(name.encode()), seed]).standard_normal(out[name].shape)
        drawn = base * np.exp(spread * noise) if base else spread * noise
        out[name] = __import__('jax').numpy.asarray(drawn.astype(out[name].dtype))
    for name, factor in factors.items():
        out[name] = (out[name] * factor).astype(out[name].dtype)
    return out
```

```python
from contextlib import ExitStack

import numpy as np

import concourse.bass as bass
from concourse import mybir

ALU = mybir.AluOpType
ACT = mybir.ActivationFunctionType
F32 = mybir.dt.float32
F32R = mybir.dt.float32r
U8 = mybir.dt.uint8

P = 128
D = 1024
S = 1024
KT = D // P
HALF = 512
NH = S // HALF
BLK = 128
NB = S // BLK
EPS = 1e-6
FF = 4 * D
FG = FF // D
HEADS1 = D // P
HEADS2 = 4
CONV_TILES = 4
CONV_GROUP = 64
LEVELS = 8

U_IN1 = 0
U_G1 = U_IN1 + 3 * HEADS1
U_OUT1 = U_G1 + HEADS1
U_MLP1 = U_OUT1 + KT
U_IN2 = U_MLP1 + FG * 2 * KT
U_G2 = U_IN2 + 3 * HEADS2
U_CONV = U_G2 + HEADS2
U_OUT2 = U_CONV + 3 * CONV_TILES
U_MLP2 = U_OUT2 + KT
UNITS = U_MLP2 + FG * 2 * KT

HG_ORDER = ("L3", "L4", "L5", "L6", "L7", "v", "k", "back", "kv", "T", "o", "L0", "L1", "L2")
HG_OPEN = {0: ("L0", "L1", "L2"), 1: tuple(x for x in HG_ORDER if x != "back"),
           HEADS1: tuple(x for x in HG_ORDER if x not in ("L0", "L1", "L2"))}
RET_ORDER = ("v", "kv", "o", "scores", "back", "k")
T_NORM0 = 0
T_HGRN = T_NORM0 + 2
T_HGRN2 = T_HGRN + len(HG_OPEN[0]) + len(HG_OPEN[1])
T_HGRN_END = T_HGRN2 + len(HG_ORDER) * (HEADS1 - 2) + len(HG_OPEN[HEADS1])
T_NORM1 = T_HGRN_END + 1
T_NORM2 = T_NORM1 + 2
T_RET = T_NORM2 + 4
T_CONV = T_RET + len(RET_ORDER) * HEADS2
T_NORM3 = T_CONV + 2 * CONV_TILES
T_NORM4 = T_NORM3 + 2

C_DECAY, C_XI = 0, BLK
C_ZETA, C_CHUNK = 0, 1


def hgrn_step(n, name):
    order = HG_OPEN.get(n, HG_ORDER) if isinstance(n, int) else HG_ORDER
    at = order.index(name)
    if isinstance(n, int):
        first = {0: T_HGRN, 1: T_HGRN + len(HG_OPEN[0])}.get(n, T_HGRN2 + len(HG_ORDER) * (n - 2))
        return first + at, (first + at) % 2
    return n * len(HG_ORDER) + (T_HGRN2 - 2 * len(HG_ORDER) + at), (T_HGRN2 + at) % 2


def ret_step(n, name):
    at = RET_ORDER.index(name)
    pair = at % 2
    if name in ("scores", "k"):
        at -= len(RET_ORDER) - 2
        if isinstance(n, int) and n == 0:
            at = ("scores", "k").index(name)
    else:
        at += 2
        if isinstance(n, int) and n == HEADS2 - 1 and name == "back":
            at -= 1
    return n * len(RET_ORDER) + (T_RET + at), pair


def build(nc, stream, x_t, gains, conv_w, lower_bound, head_rows, head_scalars, rope, ident_in, ones_in, masks_in, out_t):
    with ExitStack() as ctx:
        cursor = [(nc.sbuf_base + 63) // 64 * 64]

        def place(name, shape, dtype=F32, at=None):
            size = int(np.prod(shape[1:])) * (1 if dtype == U8 else 4)
            if at is None:
                at = cursor[0]
                cursor[0] += (size + 31) // 32 * 32
            return nc.alloc_sbuf_tensor_at(name, shape, dtype, offset=at)

        def room(size):
            at = cursor[0]
            cursor[0] += size
            return at

        def sem(name):
            return ctx.enter_context(nc.semaphore(name))

        KB = 1024
        at_x, at_r0, at_r1 = room(32 * KB), room(64 * KB), room(64 * KB)
        x_res = place("x_res", [P, KT, S], at=at_x)
        x_in = place("x_in", [P, KT, S], at=at_x)
        hi = [place(f"operand{r}_hi", [P, KT, S], F32R, at=a) for r, a in enumerate((at_r0, at_r1))]
        lo = [place(f"operand{r}_lo", [P, KT, S], F32R, at=a + 32 * KB) for r, a in enumerate((at_r0, at_r1))]
        w_raw = place("w_raw", [P, 2, KT, P])
        w_hi = place("w_hi", [P, 2, KT, P], F32R)
        w_lo = place("w_lo", [P, 2, KT, P], F32R)

        inv_rms = place("inv_rms", [P, S])
        at_sum = room(4 * KB + 64)
        sq_sum = place("sq_sum", [P, NH, HALF], at=at_sum)
        g_in = place("g_in", [P, NH, HALF], at=at_sum)
        conv_u = place("conv_u", [P, S + 2], at=at_sum)
        at_work = room(8 * KB)
        work = place("work", [P, 4, HALF], at=at_work)
        o_keep = place("o_keep", [P, S], at=at_work)
        o_sq = place("o_sq", [P, S], at=at_work + 4 * KB)
        wide_rms = place("conv_rms", [P, NB, P], at=at_work + 4 * KB)
        at_sig = room(4 * KB)
        sig = place("sig", [P, NH, HALF], at=at_sig)
        sq_sum_g = place("sq_sum_g", [P, NH, HALF], at=at_sig)
        masks_f32 = place("masks_f32", [P, 2, LEVELS - 1, BLK], at=at_r1)
        ident = place("ident", [P, P])
        ones = place("ones", [P, 3])
        gain = place("gain", [P, 9, KT])
        lb = place("lb", [P, 5, KT])
        cw = place("cw", [P, 3, CONV_TILES])
        tok_rms = place("tok_rms", [P, 2, NB, 2])
        G_MIX1, G_MLP1, G_MIX2, G_MLP2, G_FINAL, G_OUT1, G_OUT2, G_END1, G_END1_MIX2 = range(9)

        ho = place("hgrn_o", [P, KT, S], at=at_r1)
        a = at_r1 + 32 * KB
        h_qk = [place(f"hgrn_qk{b}", [P, 2, S], at=a + b * 16 * KB) for b in range(2)]
        h_q, h_k = [t[:, 0] for t in h_qk], [t[:, 1] for t in h_qk]
        h_s = place("hgrn_scores", [P, NB, BLK], at=a + 24 * KB)
        a = at_x
        h_d = [place("hgrn_f", [P, S], at=a)]
        b = a + 4 * KB
        for n in range(1, LEVELS):
            h_d.append(place(f"hgrn_decay{2 ** n}", [P, S >> n], at=b))
            b += max((S >> n) * 4, 32)
        h_v_t = place("hgrn_v_t", [P, S], at=a + 8 * KB)
        h_v = place("hgrn_v", [P, NB, P], at=a + 12 * KB)
        h_k_t = place("hgrn_k_t", [P, NB, P], at=a + 16 * KB)
        h_state = place("hgrn_state", [P, NB, P], at=a + 20 * KB)
        h_mix = place("hgrn_mixed", [P, NB // 2, BLK], at=a + 24 * KB)
        masks = place("masks", [P, 2, LEVELS - 1, BLK], U8, at=a + 28 * KB)

        ro = place("ret_o", [P, HEADS2, S], at=at_r1)
        a = at_r1 + 16 * KB
        r_s = place("ret_scores", [P, NB, BLK], at=a)
        r_k_t = place("ret_k_t", [P, NB, P], at=a + 4 * KB)
        r_v = place("ret_v", [P, NB, P], at=a + 8 * KB)
        r_state = place("ret_state", [P, NB, P], at=a + 12 * KB)
        a = at_r1 + 32 * KB
        r_q = place("ret_q", [P, S], at=a)
        r_k = place("ret_k", [P, S], at=a + 4 * KB)
        r_cos = place("ret_cos", [P, S], at=a + 8 * KB)
        r_sin = place("ret_sin", [P, S], at=a + 12 * KB)
        r_qx = place("ret_q_xi", [P, S], at=a + 16 * KB)
        r_v_t = place("ret_v_t", [P, S], at=a + 20 * KB)
        r_c = place("ret_rows", [P, HEADS2, 2 * BLK], at=a + 24 * KB)
        r_rms = place("end1_inv_rms", [P, S], at=a + 28 * KB)
        r_c1 = place("ret_scalars", [P, HEADS2, 2])

        prod_ps = ctx.enter_context(nc.psum_tensor("prod_ps", [P, 4, HALF], F32))
        side_ps = ctx.enter_context(nc.psum_tensor("side_ps", [P, 2, S], F32))

        w_landed = [sem("w_landed0"), sem("w_landed1")]
        high_begun = sem("high_begun")
        high_made = sem("high_made")
        w_split = sem("w_split")
        tiles_used = sem("tiles_used")
        prod = sem("prod")
        evac = sem("evac")
        side_done = sem("side_done")
        side_taken = sem("side_taken")
        gains_in = sem("gains_in")
        params_in = sem("params_in")
        tables_in = sem("tables_in")
        ret_consts_in = sem("ret_consts_in")
        x_landed = [[sem(f"x{half}_landed{k}") for k in range(KT)] for half in range(NH)]
        x_again = [sem(f"x_again{k}") for k in range(KT)]
        u_ready = sem("u_ready")
        u_high = sem("u_high")
        sq_ready = sem("sq_ready")
        norm_sum = sem("norm_sum")
        var_ready = sem("var_ready")
        root_ready = sem("root_ready")
        sq_added = sem("sq_added")
        h_high = sem("h_high")
        h_ready = sem("h_ready")
        q_sig, gates, g_sig = sem("q_sig"), sem("gates"), sem("g_sig")
        qk_ready = sem("qk_ready")
        level_mixed = sem("level_mixed")
        level_fed = sem("level_fed")
        rms_paired = sem("rms_paired")
        rms_widened = sem("rms_widened")
        states_ready = sem("states_ready")
        o_kept = sem("o_kept")
        o_normed = sem("o_normed")
        o_squared = sem("o_squared")
        v_t_ready = sem("v_t_ready")
        y_full = sem("y_full")
        heads_done = sem("heads_done")
        final_tile = sem("final_tile")
        stored = sem("stored")
        lb_step = sem("lb_step")

        one_norm = tok_rms[:, 0, :, 0]

        def half_chunks(half):
            return range(half * NB // 2, (half + 1) * NB // 2)

        LAST_ORDER = [(m, half) for m in range(KT - 2) for half in range(NH)]
        LAST_ORDER += [(m, half) for half in range(NH) for m in (KT - 2, KT - 1)]

        block = ctx.enter_context(nc.Block())

        @block.sync
        def _(sp):
            def load_unit(u, slot):
                sp.dma_start(w_raw[:, slot], stream[bass.ds(u, 1)].rearrange("u p k m -> (u p) k m")
                             ).then_inc(w_landed[slot], 16)

            def load_units(first, end):
                with sp.Fori(first // 2, end // 2) as i:
                    for slot in range(2):
                        sp.wait_ge(w_split, i * 2 + (slot - 1))
                        load_unit(i * 2 + slot, slot)

            load_unit(0, 0)
            for half in range(NH):
                for k in range(KT):
                    tok = slice(half * HALF, (half + 1) * HALF)
                    sp.dma_start(x_in[:, k, tok], x_t[k, :, tok]).then_inc(x_landed[half][k], 16)
                    if half == 0 and k == 3:
                        load_unit(1, 1)
            sp.dma_start(ones[:], ones_in).then_inc(tables_in, 16)
            sp.dma_start(ident[:], ident_in).then_inc(tables_in, 16)
            sp.dma_start(masks_f32[:], masks_in).then_inc(tables_in, 16)
            load_units(2, U_OUT1 - 2)
            sp.wait_ge(heads_done, 1)
            for k in range(KT):
                u = U_OUT1 - 2 + k
                sp.wait_ge(w_split, u - 1)
                load_unit(u, u % 2)
                sp.dma_start(x_res[:, k], x_t[k]).then_inc(x_again[k], 16)
            load_units(U_OUT1 - 2 + KT, UNITS)
            for half in range(NH):
                for k in range(KT):
                    tok = slice(half * HALF, (half + 1) * HALF)
                    sp.wait_ge(final_tile, half * KT + k + 1)
                    sp.dma_start(out_t[k, :, tok], x_res[:, k, tok]).then_inc(stored, 16)
            sp.wait_ge(stored, 16 * NH * KT)

        @block.gpsimd
        def _(pool):
            def split_unit(u, slot):
                pool.wait_ge(w_landed[slot], (u - slot) * 8 + 16)
                if not (isinstance(u, int) and u < 2):
                    pool.wait_ge(prod, u * 2 - 2)
                pool.sem_inc(high_begun, 1)
                nc.gpsimd.tensor_copy(w_hi[:, slot], w_raw[:, slot]).then_inc(high_made, 1)
                pool.wait_ge(high_made, u + 1)
                nc.gpsimd.tensor_tensor(w_lo[:, slot], w_raw[:, slot], w_hi[:, slot].bitcast(F32),
                                        ALU.subtract).then_inc(w_split, 1)

            def split_after_late_start(u, slot, seen):
                pool.wait_ge(w_landed[slot], (u - slot) * 8 + 16)
                pool.wait_ge(tiles_used, seen)
                early, last = slice(0, KT - 1), slice(KT - 1, KT)
                nc.gpsimd.tensor_copy(w_hi[:, slot, early], w_raw[:, slot, early])
                pool.drain()
                nc.gpsimd.tensor_tensor(w_lo[:, slot, early], w_raw[:, slot, early],
                                        w_hi[:, slot, early].bitcast(F32), ALU.subtract)
                pool.wait_ge(prod, u * 2 - 2)
                nc.gpsimd.tensor_copy(w_hi[:, slot, last], w_raw[:, slot, last]).then_inc(high_made, 1)
                pool.drain()
                nc.gpsimd.tensor_tensor(w_lo[:, slot, last], w_raw[:, slot, last],
                                        w_hi[:, slot, last].bitcast(F32), ALU.subtract).then_inc(w_split, 1)

            def split_units(first, end):
                with pool.Fori(first // 2, end // 2) as i:
                    for slot in range(2):
                        split_unit(i * 2 + slot, slot)

            split_unit(0, 0)
            split_unit(1, 1)
            split_units(2, U_OUT1 + 2)
            split_after_late_start(U_OUT1 + 2, 0, 1)
            split_after_late_start(U_OUT1 + 3, 1, 2)
            split_units(U_OUT1 + 4, U_OUT2 + 2)
            split_after_late_start(U_OUT2 + 2, 0, 3)
            split_after_late_start(U_OUT2 + 3, 1, 4)
            split_units(U_OUT2 + 4, UNITS)

        @block.tensor
        def _(pe):
            def begin(u, slot, half):
                if half == 0:
                    pe.wait_ge(w_split, u + 1)
                if not (isinstance(u, int) and u < 2):
                    pe.wait_ge(evac, u * 2 + (half - 3))

            def tiles(slot, half, region, ks, count=None):
                bank = 2 * slot + half
                act = slice(half * HALF, (half + 1) * HALF)
                for k in ks:
                    if count is not None:
                        pe.wait_ge(*count(k, half))
                    w_h, w_l = w_hi[:, slot, k], w_lo[:, slot, k]
                    a_h, a_l = hi[region][:, k, act], lo[region][:, k, act]
                    nc.tensor.matmul(prod_ps[:, bank], w_h, a_h, start=(k == 0), stop=False)
                    nc.tensor.matmul(prod_ps[:, bank], w_h, a_l, start=False, stop=False)
                    last = nc.tensor.matmul(prod_ps[:, bank], w_l, a_h, start=False, stop=(k == KT - 1))
                return last

            def product(u, slot, half, region, count=None, mid=None):
                begin(u, slot, half)
                tiles(slot, half, region, range(KT // 2), count)
                if mid is not None:
                    mid()
                tiles(slot, half, region, range(KT // 2, KT), count).then_inc(prod, 1)

            def by_tile_then_half(ready, before):
                return lambda k, half: (ready, before + (2 * k + half + 1))

            def late_start(u, region, count, after):
                for b in range(4):
                    begin(u + b // 2, b // 2, b % 2)
                    last = tiles(b // 2, b % 2, region, range(KT - 1), count)
                    if b % 2:
                        last.then_inc(tiles_used, 1)
                    for step in after[b]:
                        step()
                for b in range(4):
                    tiles(b // 2, b % 2, region, [KT - 1], count).then_inc(prod, 1)

            def units(u0, pairs, region, first=0):
                with pe.Fori(first, pairs) as j:
                    for slot in range(2):
                        for half in range(NH):
                            product(j * 2 + (u0 + slot), slot, half, region)

            def all_taken(t):
                if not (isinstance(t, int) and t < 1):
                    pe.wait_ge(side_taken, t)

            def one_back(t):
                if not (isinstance(t, int) and t < 2):
                    pe.wait_ge(side_taken, t - 1)

            def blocks_128(pair, lhs, rhs, n=NB):
                for c in range(n):
                    mm = nc.tensor.matmul(side_ps[:, pair, c * BLK:(c + 1) * BLK], lhs(c), rhs(c),
                                          start=True, stop=True)
                mm.then_inc(side_done, 1)

            def turn(pair, src, chunks=range(NB)):
                for c in chunks:
                    mm = nc.tensor.transpose(side_ps[:, pair, c * BLK:(c + 1) * BLK],
                                             src[:, c * BLK:(c + 1) * BLK], ident[:])
                mm.then_inc(side_done, 1)

            def outputs(pair, v, scores, state, q):
                for c in range(NB):
                    dst = side_ps[:, pair, c * BLK:(c + 1) * BLK]
                    mm = nc.tensor.matmul(dst, scores[:, c], v[:, c], start=True, stop=(c == 0))
                    if c > 0:
                        mm = nc.tensor.matmul(dst, q[:, c * BLK:(c + 1) * BLK], state[:, c],
                                              start=False, stop=True)
                mm.then_inc(side_done, 1)

            def sums(pair, squares, groups=slice(0, 1), chunks=range(NB)):
                n = groups.stop - groups.start
                for c in chunks:
                    mm = nc.tensor.matmul(side_ps[:, pair, c * n:(c + 1) * n], squares[:, c * BLK:(c + 1) * BLK],
                                          ones[:, groups], start=True, stop=True)
                mm.then_inc(side_done, 1)

            def spread(pair, which=0, wide=None, chunks=range(NB)):
                for c in chunks:
                    src = tok_rms[:, which, c, 0:1].to_broadcast([P, P]) if wide is None else wide[:, c]
                    mm = nc.tensor.transpose(side_ps[:, pair, c * BLK:(c + 1) * BLK], src, ident[:])
                mm.then_inc(side_done, 1)

            flat_sum = sq_sum[:].rearrange("p h t -> p (h t)")
            flat_sum_g = sq_sum_g[:].rearrange("p h t -> p (h t)")

            def norm_sums(t, count, total=flat_sum, chunks=range(NB)):
                all_taken(t)
                pe.wait_ge(norm_sum, count)
                sums(t % 2, total, chunks=chunks)

            def norm_spread(t, roots, which=0, chunks=range(NB)):
                all_taken(t)
                pe.wait_ge(root_ready, roots)
                spread(t % 2, which, chunks=chunks)

            def stage_start(u, region, count, t_norm, sums_count, roots):
                product(u, 0, 0, region, count)
                norm_sums(t_norm, sums_count)
                product(u, 0, 1, region, count)
                norm_spread(t_norm + 1, roots)
                product(u + 1, 1, 0, region)
                product(u + 1, 1, 1, region)

            def hgrn_iteration(n, par, mid_start=False):
                static = isinstance(n, int)
                project, attend, older = not (static and n == HEADS1), not (static and n == 0), \
                    not (static and n < 2)
                head, prev = n - 1, 1 - par

                def level(number, h, b):
                    t, pair = hgrn_step(n, f"L{number}")
                    one_back(t)
                    if number == 0:
                        pe.wait_ge(qk_ready, h + 1)
                        blocks_128(pair, lambda c: h_k[b][:, c * BLK:(c + 1) * BLK],
                                   lambda c: h_q[b][:, c * BLK:(c + 1) * BLK])
                        return
                    pe.wait_ge(level_mixed, h * (LEVELS - 1) + number)
                    size = (1 << number) // 2
                    for j in range(NB // 2):
                        moving = bass.AP(tensor=h_qk[b], offset=2 * j * BLK + size,
                                         ap=[[2 * S, P], [S + BLK - size, 2], [2 * size, BLK // (2 * size)],
                                             [1, size]])
                        mm = nc.tensor.matmul(side_ps[:, pair, j * BLK:(j + 1) * BLK], h_mix[:, j], moving,
                                              start=True, stop=True)
                    mm.then_inc(side_done, 1)

                def older_levels(number):
                    return lambda: attend and level(number, head, prev)

                def level7_and_v():
                    if attend:
                        level(7, head, prev)
                        t, pair = hgrn_step(n, "v")
                        one_back(t)
                        pe.wait_ge(v_t_ready, n)
                        turn(pair, h_v_t)

                def turn_k_and_back():
                    if attend:
                        t, pair = hgrn_step(n, "k")
                        one_back(t)
                        pe.wait_ge(level_fed, head * LEVELS + LEVELS)
                        turn(pair, h_k[prev])
                    if older:
                        t, pair = hgrn_step(n, "back")
                        one_back(t)
                        pe.wait_ge(o_normed, n - 1)
                        turn(pair, o_keep)

                def chunk_kv():
                    if attend:
                        t, pair = hgrn_step(n, "kv")
                        all_taken(t)
                        blocks_128(pair, lambda c: h_k_t[:, c], lambda c: h_v[:, c], NB - 1)

                def turn_scores():
                    if attend:
                        t, pair = hgrn_step(n, "T")
                        one_back(t)
                        turn(pair, h_s[:].rearrange("p c t -> p (c t)"), range(1, NB, 2))

                def out():
                    if attend:
                        t, pair = hgrn_step(n, "o")
                        all_taken(t)
                        pe.wait_ge(states_ready, n)
                        outputs(pair, h_v, h_s, h_state, h_q[prev])

                def after_fifth():
                    if project:
                        level(0, n, par)

                def newer_levels(number):
                    return lambda: project and level(number, n, par)

                u = n * 3
                slots = [(u + j // 2, (par + j // 2) % 2, j % 2) for j in range(6)]
                mids = [older_levels(3), older_levels(5), level7_and_v, chunk_kv, out, newer_levels(1)]
                ends = [older_levels(4), older_levels(6), turn_k_and_back, turn_scores, after_fifth, newer_levels(2)]
                for j, (uu, slot, half) in enumerate(slots):
                    if mid_start and j < 4:
                        continue
                    product(uu, slot, half, 0, mid=mids[j])
                    ends[j]()

            def x_count(k, half):
                return u_ready, half * KT + k + 1

            begin(0, 0, 0)
            tiles(0, 0, 0, range(KT), x_count).then_inc(prod, 1)
            begin(1, 1, 0)
            tiles(1, 0, 0, range(KT))
            tiles(0, 1, 0, range(KT), x_count).then_inc(prod, 1)
            pe.wait_ge(tables_in, 16 * 3)
            norm_sums(T_NORM0, 1)
            tiles(1, 1, 0, range(KT // 2))
            norm_spread(T_NORM0 + 1, 1)
            tiles(1, 1, 0, range(KT // 2, KT)).then_inc(prod, 2)
            hgrn_iteration(0, 0, mid_start=True)
            hgrn_iteration(1, 1)
            with pe.Fori(1, HEADS1 // 2) as i:
                hgrn_iteration(i * 2, 0)
                hgrn_iteration(i * 2 + 1, 1)
            hgrn_iteration(HEADS1, 0)
            product(U_G1 + 3, 1, 0, 0)
            all_taken(T_HGRN_END)
            pe.wait_ge(o_normed, HEADS1)
            turn(T_HGRN_END % 2, o_keep)
            product(U_G1 + 3, 1, 1, 0)
            units(U_G1, HEADS1 // 2, 0, 2)

            late_start(U_OUT1, 1, by_tile_then_half(u_ready, 16), [[]] * 4)
            units(U_OUT1, KT // 2, 1, 1)

            def mlp(u0, before, h_before, t_norm, count, roots, left=0):
                stage_start(u0, 0, by_tile_then_half(u_ready, before), t_norm, count, roots)
                units(u0, KT // 2, 0, 1)

                def down(u, h_seen):
                    for half in range(NH):
                        product(u, 0, half, 1, by_tile_then_half(h_ready, h_seen))
                    for half in range(NH):
                        product(u + 1, 1, half, 1)

                down(u0 + KT, h_before)
                units(u0 + KT, KT // 2, 1, 1)

                def group(g, left=0):
                    with pe.Fori(0, KT // 2) as j:
                        for slot in range(2):
                            for half in range(NH):
                                product(j * 2 + (g * (2 * KT) + (u0 + slot)), slot, half, 0)
                    down(g * (2 * KT) + (u0 + KT), g * (2 * KT) + h_before)
                    with pe.Fori(1, KT // 2 - left) as j:
                        for slot in range(2):
                            for half in range(NH):
                                product(j * 2 + (g * (2 * KT) + (u0 + KT + slot)), slot, half, 1)

                with pe.Fori(1, FG - 1) as g:
                    group(g)
                group(FG - 1, left)

            mlp(U_MLP1, 32, 0, T_NORM1, 2, HEADS1 + 2)

            def ret_old(n, name):
                t, pair = ret_step(n, name)
                all_taken(t)
                if name == "v":
                    pe.wait_ge(v_t_ready, n + (HEADS1 + 1))
                    turn(pair, r_v_t)
                elif name == "kv":
                    blocks_128(pair, lambda c: r_k_t[:, c], lambda c: r_v[:, c], NB - 1)
                elif name == "o":
                    pe.wait_ge(states_ready, n + (HEADS1 + 1))
                    outputs(pair, r_v, r_s, r_state, r_qx)
                else:
                    pe.wait_ge(o_normed, n + (HEADS1 + 1))
                    turn(pair, o_keep)

            def ret_new(n, name):
                t, pair = ret_step(n, name)
                all_taken(t)
                if name == "scores":
                    pe.wait_ge(qk_ready, n + (HEADS1 + 1))
                    blocks_128(pair, lambda c: r_k[:, c * BLK:(c + 1) * BLK],
                               lambda c: r_q[:, c * BLK:(c + 1) * BLK])
                else:
                    turn(pair, r_k)

            def both_norms():
                pe.wait_ge(rms_paired, 1)
                norm_spread(T_NORM2 + 2, HEADS1 + 3, 1)
                spread((T_NORM2 + 3) % 2)

            def ret_iteration(n, par, first=False):
                u = n * 3 + U_IN2
                s0, s1 = par, 1 - par

                def old(name):
                    return None if first else lambda: ret_old(n - 1, name)

                count = by_tile_then_half(u_ready, 48) if first else None
                product(u, s0, 0, 0, count, mid=old("v"))
                if first:
                    norm_sums(T_NORM2, 3)
                    norm_sums(T_NORM2 + 1, 3, flat_sum_g)
                else:
                    ret_old(n - 1, "kv")
                product(u, s0, 1, 0, mid=both_norms if first else None)
                if not first:
                    ret_old(n - 1, "o")
                product(u + 1, s1, 0, 0)
                product(u + 1, s1, 1, 0)
                product(u + 2, s0, 0, 0)
                ret_new(n, "scores")
                product(u + 2, s0, 1, 0, mid=None if first else lambda: ret_old(n - 1, "back"))
                ret_new(n, "k")

            ret_iteration(0, 0, True)
            ret_iteration(1, 1)
            with pe.Fori(1, HEADS2 // 2) as i:
                ret_iteration(i * 2, 0)
                ret_iteration(i * 2 + 1, 1)
            last_head = HEADS2 - 1
            product(U_G2, 0, 0, 0, mid=lambda: ret_old(last_head, "v"))
            ret_old(last_head, "kv")
            product(U_G2, 0, 1, 0)
            ret_old(last_head, "o")
            product(U_G2 + 1, 1, 0, 0)
            product(U_G2 + 1, 1, 1, 0)
            product(U_G2 + 2, 0, 0, 0)
            ret_old(last_head, "back")
            product(U_G2 + 2, 0, 1, 0)
            for half in range(NH):
                product(U_G2 + 3, 1, half, 0)

            def conv_sums(j):
                t = T_CONV + 2 * j
                all_taken(t)
                pe.wait_ge(o_squared, HEADS1 + HEADS2 + 1 + j)
                sums(t % 2, o_sq, slice(1, 3))

            def conv_spread(j):
                t = T_CONV + 2 * j + 1
                all_taken(t)
                pe.wait_ge(rms_widened, j + 1)
                spread(t % 2, wide=wide_rms)

            for j in range(CONV_TILES):
                for part in range(3):
                    u = U_CONV + 3 * j + part
                    product(u, u % 2, 0, 0)
                    if j and part == 1:
                        conv_spread(j - 1)
                    product(u, u % 2, 1, 0, mid=(lambda: conv_sums(j - 1)) if j and part == 0 else None)

            late_start(U_OUT2, 1, by_tile_then_half(u_ready, 64),
                       [[], [lambda: conv_sums(CONV_TILES - 1)], [lambda: conv_spread(CONV_TILES - 1)], []])
            units(U_OUT2, KT // 2, 1, 1)
            roots = HEADS1 + HEADS2 + CONV_TILES + 3
            mlp(U_MLP2, 80, FG * 16, T_NORM3, 4, roots + 1, left=1)
            def end_sums(half):
                norm_sums(T_NORM4 + 2 * half, 5 + half, chunks=half_chunks(half))

            def end_spread(half):
                norm_spread(T_NORM4 + 2 * half + 1, roots + 2 + half, chunks=half_chunks(half))

            product(UNITS - 2, 0, 0, 1)
            product(UNITS - 1, 1, 0, 1)
            product(UNITS - 2, 0, 1, 1, mid=lambda: end_sums(0))
            end_spread(0)
            product(UNITS - 1, 1, 1, 1)
            end_sums(1)
            end_spread(1)

        @block.vector
        def _(dve):
            def tokens(half):
                return slice(half * HALF, (half + 1) * HALF)

            def bank(slot, half):
                return prod_ps[:, 2 * slot + half]

            def wait_prod(u, half):
                dve.wait_ge(prod, u * 2 + (half + 1))

            def taken_step(t, pair):
                dve.wait_ge(side_done, t + 1)
                return side_ps[:, pair]

            def factor(t, chunks=slice(0, NB)):
                nc.vector.tensor_scalar(one_norm[:, chunks], taken_step(t, t % 2)[:, chunks], 1.0 / D, EPS,
                                        ALU.mult, ALU.add).then_inc(side_taken, 1)
                dve.drain()
                nc.vector.reciprocal(one_norm[:, chunks], one_norm[:, chunks]).then_inc(var_ready, 1)

            def take_norm(t):
                factor(t)
                nc.vector.tensor_copy(inv_rms[:], taken_step(t + 1, (t + 1) % 2)).then_inc(side_taken, 1)
                dve.drain()

            def scaled(dst, u, slot, half):
                wait_prod(u, half)
                nc.vector.tensor_tensor(dst, bank(slot, half), inv_rms[:, tokens(half)], ALU.mult
                                        ).then_inc(evac, 1)

            nc.vector.memset(sq_sum[:], 0.0)
            dve.wait_ge(gains_in, 16)

            def add_squares(half, slot, total, count):
                dve.wait_ge(sq_ready, count)
                return nc.vector.tensor_tensor(total[:, half], total[:, half], work[:, slot], ALU.add)

            def low_part(src, m, half, region, gain_row, count):
                dve.wait_ge(u_high, count)
                nc.vector.scalar_tensor_tensor(
                    lo[region][:, m, tokens(half)], src[:, m, tokens(half)], gain[:, gain_row, m:m + 1],
                    hi[region][:, m, tokens(half)].bitcast(F32), ALU.mult, ALU.subtract
                ).then_inc(u_ready, 1)

            for half in range(NH):
                for k in range(KT):
                    n = half * KT + k
                    low_part(x_in, k, half, 0, G_MIX1, n + 1)
                    if n:
                        dve.wait_ge(sq_added, n)
                    else:
                        dve.drain()
                    add_squares(half, n % 4, sq_sum, n + 1).then_inc(sq_added, 1)
            dve.drain()
            dve.sem_inc(norm_sum, 1)
            dve.wait_ge(params_in, 16 * 3)
            nc.vector.tensor_tensor(lb[:, 1], lb[:, 0], lb[:, 0], ALU.subtract).then_inc(lb_step, 1)
            factor(T_NORM0)
            dve.wait_ge(lb_step, 2)
            nc.vector.reciprocal(lb[:, 3], lb[:, 2])
            dve.drain()
            nc.vector.tensor_tensor(lb[:, 2], lb[:, 2], lb[:, 3], ALU.mult)
            dve.drain()
            nc.vector.tensor_tensor(lb[:, 3], lb[:, 2], lb[:, 2], ALU.subtract)
            dve.drain()
            nc.vector.tensor_scalar(lb[:, 4], lb[:, 3], -1.0, 1.0, ALU.mult, ALU.add)
            nc.vector.tensor_copy(inv_rms[:], taken_step(T_NORM0 + 1, (T_NORM0 + 1) % 2)).then_inc(side_taken, 1)
            dve.wait_ge(tables_in, 16 * 3)
            nc.vector.tensor_copy(masks[:], masks_f32[:])
            nc.vector.tensor_tensor(gain[:, G_END1_MIX2], gain[:, G_END1], gain[:, G_MIX2], ALU.mult)
            dve.drain()

            def gate_take(u0, h, half):
                scaled(g_in[:, half], u0 + h, (u0 + h) % 2, half)

            def gate_mul(o, gain_row, h, half, count):
                dve.wait_ge(g_sig, count)
                nc.vector.scalar_tensor_tensor(g_in[:, half], g_in[:, half], gain[:, gain_row, h:h + 1],
                                               sig[:, half], ALU.mult, ALU.mult)
                dve.drain()
                nc.vector.tensor_tensor(g_in[:, half], g_in[:, half], o[:, h, tokens(half)], ALU.mult
                                        ).then_inc(y_full, 1)

            def gate_low(h, half, count):
                dve.wait_ge(u_high, count)
                nc.vector.tensor_tensor(lo[1][:, h, tokens(half)], g_in[:, half],
                                        hi[1][:, h, tokens(half)].bitcast(F32), ALU.subtract
                                        ).then_inc(u_ready, 1)

            def norm_factor(count):
                dve.wait_ge(o_squared, count)
                nc.vector.tensor_reduce(one_norm, o_sq[:].rearrange("p (c v) -> p c v", c=NB),
                                        mybir.AxisListType.X, ALU.add)
                dve.drain()
                nc.vector.tensor_scalar(one_norm, one_norm, 1.0 / P, EPS, ALU.mult, ALU.add)
                dve.drain()
                nc.vector.reciprocal(one_norm, one_norm).then_inc(var_ready, 1)

            def normed(roots):
                dve.wait_ge(root_ready, roots)
                o = o_keep[:].rearrange("p (c v) -> p c v", c=NB)
                nc.vector.tensor_tensor(o, o, tok_rms[:, 0, :, 0:1].to_broadcast([P, NB, P]), ALU.mult
                                        ).then_inc(o_normed, 1)

            def hgrn_iteration(n, par):
                static = isinstance(n, int)
                gates_now, attend, older = static and n == HEADS1, not (static and n == 0), \
                    not (static and n < 2)
                project, prev = not gates_now, 1 - par
                u = n * 3

                def take(name):
                    return taken_step(*hgrn_step(n, name))

                def grow(b, number):
                    if number == 0:
                        nc.vector.tensor_tensor(h_q[b], h_q[b], h_d[0][:], ALU.mult
                                                ).then_inc(level_fed, 1)
                        return
                    h = 1 << (number - 1)
                    pairs = S // (2 * h)
                    dec = h_d[number - 1][:].rearrange("p (n two) -> p n two", two=2)
                    q2, k2 = (x.rearrange("p (n two h) -> p n two h", two=2, h=h) for x in (h_q[b], h_k[b]))
                    nc.vector.tensor_tensor(q2[:, :, 1], q2[:, :, 1],
                                            dec[:, :, 0:1].to_broadcast([P, pairs, h]), ALU.mult)
                    nc.vector.tensor_tensor(k2[:, :, 0], k2[:, :, 0],
                                            dec[:, :, 1:2].to_broadcast([P, pairs, h]), ALU.mult
                                            ).then_inc(level_fed, 1)
                    nc.vector.tensor_tensor(h_d[number][:], dec[:, :, 0], dec[:, :, 1], ALU.mult)
                    dve.drain()

                def level(b, number):
                    scores = take(f"L{number}").rearrange("p (c t) -> p c t", c=NB)
                    grow(b, number)
                    if number == 0:
                        nc.vector.tensor_tensor(h_s[:], scores, ident[:].unsqueeze(1).to_broadcast(
                            [P, NB, BLK]), ALU.mult).then_inc(side_taken, 1)
                    else:
                        h, pairs = 1 << (number - 1), BLK >> number
                        for odd in range(2):
                            block = 1 - odd
                            kept, mask = (x.rearrange(f"p {y} (n two h) -> p {y} n two h", two=2, h=h)[:, :, :, block]
                                          for x, y in ((h_s[:, odd::2], "j"),
                                                       (masks[:, odd, number - 1:number], "j")))
                            new = scores[:, 0:NB // 2, odd * (BLK // 2):(odd + 1) * (BLK // 2)]
                            last = nc.vector.copy_predicated(
                                kept, mask.to_broadcast([P, NB // 2, pairs, h]),
                                new.rearrange("p j (n h) -> p j n h", h=h))
                        last.then_inc(side_taken, 1)
                    dve.drain()

                def older_level(number):
                    if attend:
                        level(prev, number)

                def group(j):
                    if gates_now:
                        gate_take(U_G1, j // 2, j % 2)
                        return
                    dst = (h_q[par], h_k[par], h_v_t)[j // 2]
                    scaled(dst[:, tokens(j % 2)], u + j // 2, (par + j // 2) % 2, j % 2)

                def second(j):
                    if gates_now:
                        gate_mul(ho, G_OUT1, j // 2, j % 2, j + 1)
                    elif j < 2:
                        dve.wait_ge(q_sig, n * 2 + (j + 1))
                        q = h_q[par][:, tokens(j)]
                        nc.vector.scalar_tensor_tensor(q, q, float(P) ** -0.5, sig[:, j], ALU.mult, ALU.mult)

                def third(j):
                    if gates_now:
                        gate_low(j // 2, j % 2, 16 + j + 1)

                older_level(3)
                group(0)
                older_level(4)
                if older:
                    norm_factor(n - 1)
                second(0)
                older_level(5)
                group(1)
                third(0)
                older_level(6)
                if older:
                    normed(n)
                second(1)
                older_level(7)
                if attend:
                    nc.vector.tensor_copy(h_v[:].rearrange("p c v -> p (c v)"), take("v")).then_inc(side_taken, 1)
                group(2)
                third(1)
                if attend:
                    nc.vector.tensor_copy(h_k_t[:].rearrange("p c k -> p (c k)"), take("k")
                                          ).then_inc(side_taken, 1)
                if older:
                    o_at = ho[:, n - 2] if static else ho[:, bass.ds(n - 2, 1)].rearrange("p a s -> p (a s)")
                    nc.vector.tensor_copy(o_at, take("back")).then_inc(side_taken, 1)
                second(2)
                if attend:
                    kv = take("kv").rearrange("p (c v) -> p c v", c=NB)
                    nc.vector.tensor_copy(h_state[:, 1], kv[:, 0])
                    for c in range(1, NB - 1):
                        dve.drain()
                        last = nc.vector.scalar_tensor_tensor(
                            h_state[:, c + 1], h_state[:, c], h_d[LEVELS - 1][:, c:c + 1], kv[:, c],
                            ALU.mult, ALU.add)
                    last.then_inc(side_taken, 1)
                    dve.drain()
                    dve.sem_inc(states_ready, 1)
                group(3)
                if attend:
                    turned = take("T").rearrange("p (c t) -> p c t", c=NB)
                    nc.vector.tensor_copy(h_s[:, 1::2], turned[:, 1::2]).then_inc(side_taken, 1)
                third(2)
                second(3)
                if project:
                    dve.wait_ge(gates, n * 2 + 2)
                    at = slice(n, n + 1) if static else bass.ds(n, 1)
                    nc.vector.tensor_scalar(h_d[0][:], h_d[0][:], lb[:, 4, at], lb[:, 3, at], ALU.mult, ALU.add)
                    nc.vector.tensor_scalar(h_k[par], h_k[par], lb[:, 4, at], None, ALU.mult
                                            ).then_inc(qk_ready, 1)
                    dve.drain()
                if attend:
                    nc.vector.tensor_copy(o_keep[:], take("o")).then_inc(side_taken, 1)
                    dve.drain()
                    dve.sem_inc(o_kept, 1)
                group(4)
                third(3)
                if project:
                    level(par, 0)
                second(4)
                if project:
                    level(par, 1)
                if gates_now:
                    norm_factor(n)
                group(5)
                third(4)
                second(5)
                third(5)
                if project:
                    dve.drain()
                    dve.sem_inc(v_t_ready, 1)
                    level(par, 2)
                if gates_now:
                    normed(n + 1)

            hgrn_iteration(0, 0)
            hgrn_iteration(1, 1)
            with dve.Fori(1, HEADS1 // 2) as i:
                hgrn_iteration(i * 2, 0)
                hgrn_iteration(i * 2 + 1, 1)
            hgrn_iteration(HEADS1, 0)

            def gate(u0, o, gain_row, h, half, g_before, high_before):
                gate_take(u0, h, half)
                gate_mul(o, gain_row, h, half, g_before + 2 * h + half + 1)
                gate_low(h, half, high_before + 2 * h + half + 1)

            gate_take(U_G1, 3, 0)
            nc.vector.tensor_copy(ho[:, HEADS1 - 1], taken_step(T_HGRN_END, T_HGRN_END % 2)
                                  ).then_inc(side_taken, 1)
            dve.drain()
            dve.sem_inc(heads_done, 1)
            gate_mul(ho, G_OUT1, 3, 0, 7)
            gate_low(3, 0, 16 + 7)
            gate(U_G1, ho, G_OUT1, 3, 1, 0, 16)
            for h in range(4, HEADS1):
                for half in range(NH):
                    gate(U_G1, ho, G_OUT1, h, half, 0, 16)

            def advance(u0, make_operand, gain_row, high_before, sq_before, reload=False, with_gain=False):
                dve.drain()
                nc.vector.memset(sq_sum[:], 0.0)
                if with_gain:
                    nc.vector.memset(sq_sum_g[:], 0.0)

                def finish(m, half):
                    n = 2 * m + half + 1
                    if make_operand:
                        low_part(x_res, m, half, 0, gain_row, high_before + n)
                    if with_gain:
                        add_squares(half, 2 * (n % 2), sq_sum, sq_before + 2 * n - 1)
                        add_squares(half, 2 * (n % 2) + 1, sq_sum_g, sq_before + 2 * n)
                    else:
                        add_squares(half, 2 * (n % 2), sq_sum, sq_before + n)

                for m in range(KT):
                    for half in range(NH):
                        wait_prod(u0 + m, half)
                        if reload and half == 0:
                            dve.wait_ge(x_again[m], 16)
                        nc.vector.tensor_tensor(x_res[:, m, tokens(half)], bank(m % 2, half),
                                                x_res[:, m, tokens(half)], ALU.add).then_inc(evac, 1)
                        if m or half:
                            finish(*divmod(2 * m + half - 1, 2))
                finish(KT - 1, 1)
                dve.drain()
                dve.sem_inc(norm_sum, 1)

            advance(U_OUT1, True, G_MLP1, 32, 16, reload=True)

            def mlp(u0, h_before, t_norm, finish):
                take_norm(t_norm)

                def up(u, h_seen):
                    def low(m, half):
                        dve.wait_ge(h_high, h_seen + (2 * m + half + 1))
                        nc.vector.tensor_tensor(lo[1][:, m, tokens(half)], work[:, (2 * m + half) % 4],
                                                hi[1][:, m, tokens(half)].bitcast(F32),
                                                ALU.subtract).then_inc(h_ready, 1)

                    for m in range(KT):
                        for half in range(NH):
                            wait_prod(u + m, half)
                            nc.vector.scalar_tensor_tensor(
                                work[:, (2 * m + half) % 4], bank(m % 2, half), 0.0,
                                inv_rms[:, tokens(half)], ALU.max, ALU.mult).then_inc(evac, 1)
                            if m or half:
                                low(*divmod(2 * m + half - 1, 2))
                    low(KT - 1, 1)

                with dve.Fori(0, FG - 1) as g:
                    up(g * (2 * KT) + u0, g * (2 * KT) + h_before)
                    for m in range(KT):
                        for half in range(NH):
                            wait_prod(g * (2 * KT) + (u0 + KT + m), half)
                            nc.vector.tensor_tensor(x_res[:, m, tokens(half)], bank(m % 2, half),
                                                    x_res[:, m, tokens(half)], ALU.add).then_inc(evac, 1)
                g = FG - 1
                up(g * 2 * KT + u0, g * 2 * KT + h_before)
                finish(g * 2 * KT + u0 + KT)

            mlp(U_MLP1, 0, T_NORM1, lambda u: advance(u, True, G_END1_MIX2, 48, 32, with_gain=True))

            t = T_NORM2
            nc.vector.tensor_scalar(tok_rms[:, 0, :, 0], taken_step(t, t % 2)[:, 0:NB], 1.0 / D, EPS,
                                    ALU.mult, ALU.add).then_inc(side_taken, 1)
            dve.drain()
            nc.vector.reciprocal(tok_rms[:, 0, :, 0], tok_rms[:, 0, :, 0])
            dve.drain()
            nc.vector.scalar_tensor_tensor(tok_rms[:, 1, :, 0], taken_step(t + 1, (t + 1) % 2)[:, 0:NB], 1.0 / D,
                                           tok_rms[:, 0, :, 0], ALU.mult, ALU.mult).then_inc(side_taken, 1)
            dve.drain()
            nc.vector.tensor_scalar(tok_rms[:, 1, :, 0], tok_rms[:, 1, :, 0], EPS, None, ALU.add)
            dve.drain()
            nc.vector.reciprocal(tok_rms[:, 1, :, 0], tok_rms[:, 1, :, 0]).then_inc(var_ready, 1)
            dve.wait_ge(root_ready, HEADS1 + 3)
            nc.vector.tensor_tensor(tok_rms[:, 1, :, 0], tok_rms[:, 1, :, 0], tok_rms[:, 0, :, 0], ALU.mult
                                    ).then_inc(rms_paired, 1)
            nc.vector.tensor_copy(inv_rms[:], taken_step(t + 2, (t + 2) % 2)).then_inc(side_taken, 1)
            dve.wait_ge(ret_consts_in, 48)
            dve.drain()
            for table in (r_cos, r_sin):
                nc.vector.tensor_tensor(table[:], table[:], inv_rms[:], ALU.mult)
            nc.vector.tensor_copy(r_rms[:], taken_step(t + 3, (t + 3) % 2)).then_inc(side_taken, 1)
            dve.drain()
            lower, upper = slice(0, P // 2), slice(P // 2, P)

            def end_of_block1(*tiles):
                for m in tiles:
                    nc.vector.scalar_tensor_tensor(x_res[:, m], x_res[:, m], gain[:, G_END1, m:m + 1],
                                                   r_rms[:], ALU.mult, ALU.mult)

            def rotated(dst, u, slot, half):
                tok = tokens(half)
                wait_prod(u, half)
                nc.vector.tensor_tensor(dst[:, tok], bank(slot, half), r_cos[:, tok], ALU.mult)
                nc.vector.tensor_tensor(sig[lower, half], bank(slot, half)[upper], r_sin[upper, tok], ALU.mult)
                nc.vector.tensor_tensor(sig[upper, half], bank(slot, half)[lower], r_sin[lower, tok],
                                        ALU.mult).then_inc(evac, 1)
                dve.drain()
                nc.vector.tensor_tensor(dst[:, tok], dst[:, tok], sig[:, half], ALU.add)

            def ret_v(n):
                nc.vector.tensor_copy(r_v[:].rearrange("p c v -> p (c v)"), taken_step(*ret_step(n, "v"))
                                      ).then_inc(side_taken, 1)

            def head_const(table, n, a, b):
                return table[:, n, a:b] if isinstance(n, int) else \
                    table[:, bass.ds(n, 1), a:b].rearrange("p a s -> p (a s)")

            def ret_states(n):
                kv = taken_step(*ret_step(n, "kv")).rearrange("p (c v) -> p c v", c=NB)
                nc.vector.tensor_copy(r_state[:, 1], kv[:, 0])
                for c in range(1, NB - 1):
                    dve.drain()
                    last = nc.vector.scalar_tensor_tensor(
                        r_state[:, c + 1], r_state[:, c], head_const(r_c1, n, C_CHUNK, C_CHUNK + 1), kv[:, c],
                        ALU.mult, ALU.add)
                last.then_inc(side_taken, 1)
                dve.drain()
                dve.sem_inc(states_ready, 1)

            def ret_out(n):
                nc.vector.tensor_copy(o_keep[:], taken_step(*ret_step(n, "o"))).then_inc(side_taken, 1)
                dve.drain()
                dve.sem_inc(o_kept, 1)

            def ret_back(n):
                o_at = ro[:, n] if isinstance(n, int) else ro[:, bass.ds(n, 1)].rearrange("p a s -> p (a s)")
                nc.vector.tensor_copy(o_at, taken_step(*ret_step(n, "back"))).then_inc(side_taken, 1)

            def ret_iteration(n, par, first=False):
                u, s0, s1 = n * 3 + U_IN2, par, 1 - par
                if not first:
                    ret_v(n - 1)
                rotated(r_q, u, s0, 0)
                if not first:
                    ret_states(n - 1)
                rotated(r_q, u, s0, 1)
                if not first:
                    ret_out(n - 1)
                dve.drain()
                nc.vector.tensor_tensor(
                    r_qx[:].rearrange("p (c t) -> p c t", c=NB), r_q[:].rearrange("p (c t) -> p c t", c=NB),
                    head_const(r_c, n, C_XI, C_XI + BLK).unsqueeze(1).to_broadcast([P, NB, BLK]), ALU.mult)
                rotated(r_k, u + 1, s1, 0)
                if not first:
                    norm_factor(n + HEADS1)
                rotated(r_k, u + 1, s1, 1)
                dve.drain()
                dve.sem_inc(qk_ready, 1)
                if not first:
                    normed(n + (HEADS1 + 3))
                scaled(r_v_t[:, tokens(0)], u + 2, s0, 0)
                nc.vector.tensor_tensor(
                    r_s[:], taken_step(*ret_step(n, "scores")).rearrange("p (c t) -> p c t", c=NB),
                    head_const(r_c, n, C_DECAY, C_DECAY + BLK).unsqueeze(1).to_broadcast([P, NB, BLK]), ALU.mult
                ).then_inc(side_taken, 1)
                if not first:
                    ret_back(n - 1)
                scaled(r_v_t[:, tokens(1)], u + 2, s0, 1)
                dve.drain()
                dve.sem_inc(v_t_ready, 1)
                nc.vector.tensor_scalar(r_k_t[:].rearrange("p c k -> p (c k)"), taken_step(*ret_step(n, "k")),
                                        head_const(r_c1, n, C_ZETA, C_ZETA + 1), None, ALU.mult
                                        ).then_inc(side_taken, 1)

            ret_iteration(0, 0, True)
            ret_iteration(1, 1)
            with dve.Fori(1, HEADS2 // 2) as i:
                ret_iteration(i * 2, 0)
                ret_iteration(i * 2 + 1, 1)
            G, H, last_head = 2 * HEADS1, 64, HEADS2 - 1
            ret_v(last_head)
            gate_take(U_G2, 0, 0)
            ret_states(last_head)
            gate_mul(ro, G_OUT2, 0, 0, G + 1)
            gate_take(U_G2, 0, 1)
            gate_low(0, 0, H + 1)
            ret_out(last_head)
            gate_mul(ro, G_OUT2, 0, 1, G + 2)
            gate_take(U_G2, 1, 0)
            gate_low(0, 1, H + 2)
            norm_factor(HEADS1 + HEADS2)
            gate_mul(ro, G_OUT2, 1, 0, G + 3)
            gate_take(U_G2, 1, 1)
            normed(HEADS1 + HEADS2 + 3)
            gate_low(1, 0, H + 3)
            gate_mul(ro, G_OUT2, 1, 1, G + 4)
            gate_low(1, 1, H + 4)
            gate(U_G2, ro, G_OUT2, 2, 0, G, H)
            ret_back(last_head)
            gate(U_G2, ro, G_OUT2, 2, 1, G, H)
            for half in range(NH):
                gate(U_G2, ro, G_OUT2, 3, half, G, H)

            def conv_factor(j):
                t = T_CONV + 2 * j
                nc.vector.tensor_scalar(tok_rms[:, 0].rearrange("p c g -> p (c g)"),
                                        taken_step(t, t % 2)[:, 0:2 * NB], 1.0 / CONV_GROUP, EPS,
                                        ALU.mult, ALU.add).then_inc(side_taken, 1)
                dve.drain()
                nc.vector.reciprocal(tok_rms[:, 0], tok_rms[:, 0]).then_inc(var_ready, 1)

            def conv_widen(j):
                dve.wait_ge(root_ready, HEADS1 + HEADS2 + 4 + j)
                nc.vector.tensor_copy(wide_rms[:].rearrange("p c (g x) -> p c g x", g=2),
                                      tok_rms[:, 0].unsqueeze(3).to_broadcast([P, NB, 2, CONV_GROUP])
                                      ).then_inc(rms_widened, 1)

            def conv_y(j):
                t, tile = T_CONV + 2 * j + 1, HEADS2 + j
                nc.vector.scalar_tensor_tensor(o_keep[:], o_keep[:], gain[:, G_OUT2, tile:tile + 1],
                                               taken_step(t, t % 2), ALU.mult, ALU.mult).then_inc(side_taken, 1)
                dve.drain()
                dve.sem_inc(y_full, 2)
                dve.wait_ge(u_high, H + 2 * (tile + 1))
                nc.vector.tensor_tensor(lo[1][:, tile], o_keep[:], hi[1][:, tile].bitcast(F32), ALU.subtract
                                        ).then_inc(u_ready, 2)
                dve.drain()

            dve.drain()
            nc.vector.memset(conv_u[:, 0:2], 0.0)
            for j in range(CONV_TILES):
                u = U_CONV + 3 * j
                scaled(conv_u[:, 2:2 + HALF], u, u % 2, 0)
                if j:
                    conv_factor(j - 1)
                scaled(conv_u[:, 2 + HALF:], u, u % 2, 1)
                end_of_block1(2 * j, 2 * j + 1)
                if j:
                    conv_widen(j - 1)
                for half in range(NH):
                    scaled(sig[:, half], u + 1, (u + 1) % 2, half)
                    dve.drain()
                    part = conv_u[:, 2 + half * HALF:2 + (half + 1) * HALF]
                    nc.vector.tensor_tensor(part, part, sig[:, half], ALU.mult)
                    if j and half == 0:
                        conv_y(j - 1)
                dve.drain()
                nc.vector.tensor_scalar(o_keep[:], conv_u[:, 0:S], cw[:, 0, j:j + 1], None, ALU.mult)
                for tap in (1, 2):
                    dve.drain()
                    nc.vector.scalar_tensor_tensor(o_keep[:], conv_u[:, tap:tap + S], cw[:, tap, j:j + 1],
                                                   o_keep[:], ALU.mult, ALU.add)
                for half in range(NH):
                    scaled(sig[:, half], u + 2, u % 2, half)
                    dve.drain()
                    nc.vector.tensor_tensor(o_keep[:, tokens(half)], o_keep[:, tokens(half)], sig[:, half],
                                            ALU.mult)
                dve.drain()
                dve.sem_inc(o_kept, 1)
            conv_factor(CONV_TILES - 1)
            conv_widen(CONV_TILES - 1)
            conv_y(CONV_TILES - 1)

            advance(U_OUT2, True, G_MLP2, 80, 64)

            def last_advance(u0):
                dve.drain()
                nc.vector.memset(sq_sum[:], 0.0)
                tokens_of = [slice(h * NB // 2, (h + 1) * NB // 2) for h in range(NH)]

                def take(n):
                    m, half = LAST_ORDER[n]
                    dve.wait_ge(prod, 2 * u0 + n + 1)
                    nc.vector.tensor_tensor(x_res[:, m, tokens(half)], bank(m % 2, half),
                                            x_res[:, m, tokens(half)], ALU.add).then_inc(evac, 1)

                def add(n):
                    if n and LAST_ORDER[n - 1][1] == LAST_ORDER[n][1]:
                        dve.drain()
                    add_squares(LAST_ORDER[n][1], 2 * ((n + 1) % 2), sq_sum, 81 + n)

                def half_summed():
                    dve.drain()
                    dve.sem_inc(norm_sum, 1)

                def finals(half, tiles):
                    t = T_NORM4 + 2 * half + 1
                    rms = taken_step(t, t % 2)[:, tokens(half)]
                    for m in tiles:
                        nc.vector.scalar_tensor_tensor(
                            x_res[:, m, tokens(half)], x_res[:, m, tokens(half)], gain[:, G_FINAL, m:m + 1],
                            rms, ALU.mult, ALU.mult).then_inc(final_tile, 1)

                before_last = 2 * KT - 2
                for n in range(before_last):
                    take(n)
                    if n:
                        add(n - 1)
                add(before_last - 1)
                half_summed()
                factor(T_NORM4, tokens_of[0])
                take(before_last)
                finals(0, range(0, 4))
                add(before_last)
                finals(0, range(4, KT - 1))
                take(before_last + 1)
                finals(0, [KT - 1])
                dve.drain()
                dve.sem_inc(side_taken, 1)
                add(before_last + 1)
                half_summed()
                factor(T_NORM4 + 2, tokens_of[1])
                finals(1, range(KT))

            mlp(U_MLP2, FG * 16, T_NORM3, last_advance)

        @block.scalar
        def _(act):
            act.dma_start(gain[:, 0:8], gains).then_inc(gains_in, 16)
            act.dma_start(lb[:, 0], lower_bound).then_inc(params_in, 16)
            act.dma_start(cw[:], conv_w).then_inc(params_in, 16)
            act.dma_start(r_c1[:], head_scalars).then_inc(params_in, 16)

            def tokens(half):
                return slice(half * HALF, (half + 1) * HALF)

            act.wait_ge(gains_in, 16)

            def high_part(src, m, half, gain_row):
                nc.scalar.activation(hi[0][:, m, tokens(half)], src[:, m, tokens(half)], ACT.Copy,
                                     scale=gain[:, gain_row, m:m + 1]).then_inc(u_high, 1)

            for half in range(NH):
                for k in range(KT):
                    n = half * KT + k
                    act.wait_ge(x_landed[half][k], 16)
                    if n >= 4:
                        act.wait_ge(sq_added, n - 3)
                    high_part(x_in, k, half, G_MIX1)
                    nc.scalar.activation(work[:, n % 4], x_in[:, k, tokens(half)], ACT.Square
                                         ).then_inc(sq_ready, 1)

            def root(count, view):
                act.wait_ge(var_ready, count)
                nc.scalar.activation(view, view, ACT.Sqrt).then_inc(root_ready, 1)

            act.wait_ge(lb_step, 1)
            nc.scalar.activation(lb[:, 2], lb[:, 1], ACT.Exp).then_inc(lb_step, 1)
            root(1, one_norm)

            def sigmoid_g(u0, h, half):
                act.wait_ge(evac, 2 * (u0 + h) + half + 1)
                nc.scalar.activation(sig[:, half], g_in[:, half], ACT.Sigmoid).then_inc(g_sig, 1)

            def high_y(h, half, y_before):
                act.wait_ge(y_full, y_before + 2 * h + half + 1)
                nc.scalar.activation(hi[1][:, h, tokens(half)], g_in[:, half], ACT.Copy).then_inc(u_high, 1)

            def squares_o(count):
                act.wait_ge(o_kept, count)
                nc.scalar.activation(o_sq[:], o_keep[:], ACT.Square).then_inc(o_squared, 1)

            def gather(b, head, number):
                h = 1 << (number - 1)
                q, k = (x.rearrange("p (j odd n two h) -> p j odd n two h", j=NB // 2, odd=2, two=2, h=h)
                        for x in (h_q[b], h_k[b]))
                mix = h_mix[:].rearrange("p j (n two h) -> p j n two h", two=2, h=h)
                act.wait_ge(level_fed, head * LEVELS + number)
                nc.scalar.activation(mix[:, :, :, 0], k[:, :, 0, :, 0], ACT.Copy)
                nc.scalar.activation(mix[:, :, :, 1], q[:, :, 1, :, 1], ACT.Copy).then_inc(level_mixed, 1)

            def hgrn_iteration(n, par, attend=True):
                g = n * 6

                def q_sigmoid(half):
                    act.wait_ge(evac, g + (half + 1))
                    nc.scalar.activation(sig[:, half], h_q[par][:, tokens(half)], ACT.Sigmoid
                                         ).then_inc(q_sig, 1)

                def older(number):
                    if attend:
                        gather(1 - par, n - 1, number)

                older(4)
                q_sigmoid(0)
                older(5)
                if not (isinstance(n, int) and n < 2):
                    root(n, one_norm)
                older(6)
                q_sigmoid(1)
                older(7)
                for half in range(NH):
                    act.wait_ge(evac, g + (half + 3))
                    nc.scalar.activation(h_d[0][:, tokens(half)], h_k[par][:, tokens(half)], ACT.Sigmoid)
                    nc.scalar.activation(h_k[par][:, tokens(half)], h_k[par][:, tokens(half)], ACT.Sigmoid,
                                         scale=-1.0).then_inc(gates, 1)
                if attend:
                    squares_o(n)
                gather(par, n, 1)
                gather(par, n, 2)
                gather(par, n, 3)

            hgrn_iteration(0, 0, attend=False)
            hgrn_iteration(1, 1)
            with act.Fori(1, HEADS1 // 2) as i:
                hgrn_iteration(i * 2, 0)
                hgrn_iteration(i * 2 + 1, 1)
            gather(1, HEADS1 - 1, 4)
            sigmoid_g(U_G1, 0, 0)
            gather(1, HEADS1 - 1, 5)
            root(HEADS1, one_norm)
            high_y(0, 0, 0)
            gather(1, HEADS1 - 1, 6)
            sigmoid_g(U_G1, 0, 1)
            gather(1, HEADS1 - 1, 7)
            high_y(0, 1, 0)
            for half in range(NH):
                sigmoid_g(U_G1, 1, half)
                high_y(1, half, 0)
            squares_o(HEADS1)
            sigmoid_g(U_G1, 2, 0)
            root(HEADS1 + 1, one_norm)
            high_y(2, 0, 0)
            sigmoid_g(U_G1, 2, 1)
            high_y(2, 1, 0)
            for h in range(3, HEADS1):
                for half in range(NH):
                    sigmoid_g(U_G1, h, half)
                    high_y(h, half, 0)

            def advance(u0, make_operand, gain_row, with_gain=False):
                for m in range(KT):
                    for half in range(NH):
                        act.wait_ge(evac, 2 * (u0 + m) + half + 1)
                        if make_operand:
                            high_part(x_res, m, half, gain_row)
                        slot = 2 * ((half + 1) % 2)
                        nc.scalar.activation(work[:, slot], x_res[:, m, tokens(half)], ACT.Square
                                             ).then_inc(sq_ready, 1)
                        if with_gain:
                            nc.scalar.activation(work[:, slot + 1], x_res[:, m, tokens(half)], ACT.Square,
                                                 scale=gain[:, G_END1, m:m + 1]).then_inc(sq_ready, 1)

            advance(U_OUT1, True, G_MLP1)

            def mlp(u0, count, finish):
                root(count, one_norm)

                def up(u):
                    for m in range(KT):
                        for half in range(NH):
                            slot = (2 * m + half) % 4
                            act.wait_ge(evac, u * 2 + (2 * m + half + 1))
                            nc.scalar.activation(work[:, slot], work[:, slot], ACT.Square)
                            act.drain()
                            nc.scalar.activation(hi[1][:, m, tokens(half)], work[:, slot], ACT.Copy
                                                 ).then_inc(h_high, 1)

                with act.Fori(0, FG - 1) as g:
                    up(g * (2 * KT) + u0)
                up((FG - 1) * 2 * KT + u0)
                finish((FG - 1) * 2 * KT + u0 + KT)

            mlp(U_MLP1, HEADS1 + 2, lambda u: advance(u, True, G_END1_MIX2, True))

            act.wait_ge(prod, 2 * U_IN2)
            act.dma_start(r_c[:], head_rows).then_inc(ret_consts_in, 16)
            act.dma_start(r_cos[:], rope[0]).then_inc(ret_consts_in, 16)
            act.dma_start(r_sin[:], rope[1]).then_inc(ret_consts_in, 16)
            root(HEADS1 + 3, tok_rms[:, :, :, 0])

            def ret_head(n):
                squares_o(n + (HEADS1 + 1))
                root(n + (HEADS1 + 4), one_norm)

            with act.Fori(0, HEADS2 - 1) as n:
                ret_head(n)
            for half in range(NH):
                sigmoid_g(U_G2, 0, half)
                high_y(0, half, 2 * HEADS1)
            squares_o(HEADS1 + HEADS2)
            sigmoid_g(U_G2, 1, 0)
            root(HEADS1 + HEADS2 + 3, one_norm)
            high_y(1, 0, 2 * HEADS1)
            sigmoid_g(U_G2, 1, 1)
            high_y(1, 1, 2 * HEADS1)
            for h in range(2, HEADS2):
                for half in range(NH):
                    sigmoid_g(U_G2, h, half)
                    high_y(h, half, 2 * HEADS1)
            for j in range(CONV_TILES):
                squares_o(HEADS1 + HEADS2 + 1 + j)
                root(HEADS1 + HEADS2 + 4 + j, tok_rms[:, 0])
                act.wait_ge(y_full, 2 * (HEADS1 + HEADS2 + 1 + j))
                nc.scalar.activation(hi[1][:, HEADS2 + j], o_keep[:], ACT.Copy).then_inc(u_high, 2)
            advance(U_OUT2, True, G_MLP2)
            roots = HEADS1 + HEADS2 + CONV_TILES + 3

            def last_squares(u0):
                for n, (m, half) in enumerate(LAST_ORDER):
                    act.wait_ge(evac, 2 * u0 + n + 1)
                    nc.scalar.activation(work[:, 2 * ((n + 1) % 2)], x_res[:, m, tokens(half)], ACT.Square
                                         ).then_inc(sq_ready, 1)
                    if m == KT - 1:
                        root(roots + 2 + half, one_norm[:, half * NB // 2:(half + 1) * NB // 2])

            mlp(U_MLP2, roots + 1, last_squares)


def level_masks():
    s, t = np.arange(BLK)[:, None], np.arange(BLK)[None, :]
    out = np.zeros((BLK, 2, LEVELS - 1, BLK), np.float32)
    for n in range(LEVELS - 1):
        h = 1 << n
        mask = (s // (2 * h) == t // (2 * h)) & (s % (2 * h) < h) & (t % (2 * h) >= h)
        out[:, 0, n], out[:, 1, n] = mask, mask.T
    return out


def retention_constants():
    scale = np.float32(P ** -0.5)
    idx = np.arange(BLK, dtype=np.float32)
    rows = np.zeros((P, HEADS2, 2 * BLK), np.float32)
    scalars = np.zeros((P, HEADS2, 2), np.float32)
    for h in range(HEADS2):
        log_gamma = np.log(np.float32(1.0) - np.float32(2.0) ** np.float32(-5.0 - h))
        diff = idx[None, :] - idx[:, None]
        rows[:, h, C_DECAY:C_DECAY + BLK] = np.where(diff >= 0, np.exp(log_gamma * np.maximum(diff, 0)), 0) * scale
        rows[:, h, C_XI:C_XI + BLK] = np.exp(log_gamma * (idx + 1))[None]
        scalars[:, h, C_ZETA] = np.exp(log_gamma * (BLK - 1 - idx)) * scale
        scalars[:, h, C_CHUNK] = np.exp(log_gamma * BLK)
    return rows, scalars


def rotary_tables():
    half = P // 2
    freq = (np.float32(1.0) / (np.float32(10000.0) ** (np.arange(half, dtype=np.float32) / np.float32(half))))
    ang = freq.astype(np.float32)[:, None] * np.arange(S, dtype=np.float32)[None]
    cos, sin = np.cos(ang).astype(np.float32), np.sin(ang).astype(np.float32)
    return np.stack([np.concatenate([cos, cos]), np.concatenate([sin, -sin])])


def unit(w, row, col):
    return w[row:row + D, col:col + P].reshape(KT, P, P).transpose(1, 0, 2)


def by_tile(v):
    return np.asarray(v).reshape(-1, P).T


def kernel(**inputs):
    from concourse import bacc
    from concourse.bass_utils import run_bass_kernel_spmd

    a = {k: np.asarray(v) for k, v in inputs.items()}
    conv = HEADS2 * P
    stream = np.empty((UNITS, P, KT, P), np.float32)
    blocks = [(a["hgrn_w_in"][0], 0, part * D + h * P) for h in range(HEADS1) for part in range(3)]
    blocks += [(a["hgrn_w_in"][0], 0, 3 * D + h * P) for h in range(HEADS1)]
    blocks += [(a["hgrn_w_out"][0], 0, m * P) for m in range(KT)]

    def mlp_blocks(w1, w2):
        for g in range(FG):
            for m in range(KT):
                yield w1, 0, g * D + m * P
            for m in range(KT):
                yield w2, g * D, m * P

    blocks += mlp_blocks(a["mlp_w1"][0], a["mlp_w2"][0])
    blocks += [(a["w_in_2"], 0, 3 * conv + part * HEADS2 * P + h * P) for h in range(HEADS2) for part in range(3)]
    blocks += [(a["w_in_2"], 0, 3 * conv + 3 * HEADS2 * P + h * P) for h in range(HEADS2)]
    blocks += [(a["w_in_2"], 0, part * conv + j * P) for j in range(CONV_TILES) for part in (1, 2, 0)]
    w_out_2 = np.concatenate([a["w_out_2"][conv:], a["w_out_2"][:conv]])
    blocks += [(w_out_2, 0, m * P) for m in range(KT)]
    blocks += mlp_blocks(a["w_up_2"], a["w_down_2"])
    for n, (w, row, col) in enumerate(blocks):
        stream[n] = unit(w, row, col)

    out_gain2 = np.concatenate([a["ret_norm_g_2"], a["conv_norm_g_2"]])
    gains = np.stack([by_tile(v) for v in (
        a["norm_mix"][0], a["norm_mlp"][0], a["norm1_g_2"], a["norm2_g_2"], a["final_norm_g_2"],
        a["hgrn_out_norm"][0], out_gain2, a["norm_final"])], axis=1)
    head_rows, head_scalars = retention_constants()
    ones = np.zeros((P, 3), np.float32)
    ones[:, 0] = 1.0
    for g in range(2):
        ones[g * CONV_GROUP:(g + 1) * CONV_GROUP, 1 + g] = 1.0
    arrays = {
        "stream": stream,
        "x_t": np.ascontiguousarray(a["x"][0].T).reshape(KT, P, S),
        "gains": np.ascontiguousarray(gains),
        "conv_w": np.ascontiguousarray(a["conv_w_2"].reshape(3, CONV_TILES, P).transpose(2, 0, 1)),
        "lower_bound": np.ascontiguousarray(by_tile(a["hgrn_lower_bound"][0])),
        "head_rows": head_rows,
        "head_scalars": head_scalars,
        "rope": rotary_tables(),
        "ident": np.eye(P, dtype=np.float32),
        "ones": ones,
        "masks": level_masks(),
    }
    nc = bacc.Bacc("TRN2", target_bir_lowering=False, num_devices=1)
    args = [nc.dram_tensor(n, v.shape, mybir.dt.from_np(v.dtype), kind="ExternalInput").ap()
            for n, v in arrays.items()]
    out_t = nc.dram_tensor("out_t", (KT, P, S), F32, kind="ExternalOutput").ap()
    build(nc, *args, out_t)
    got = run_bass_kernel_spmd(nc, [arrays], core_ids=[0]).results[0]["out_t"]
    return np.ascontiguousarray(np.asarray(got).reshape(D, S).T).reshape(1, S, D)
```
